# Optimizing a Trainium2 kernel written in Bass

```python
import math
import jax, jax.numpy as jnp
from jax import lax
import numpy as np

D_MODEL = 1024
BATCH = 1
SEQ = 128
DEPTH = 1
DEC_BATCH = 1
DEC_SEQ = 512
PAST_LEN = 128

GRID_W = 64
N_HEADS = 6
HEAD_DIM = 64
V_DIM = 2 * HEAD_DIM
ATTN_QK_WIDTH = N_HEADS * 2 * HEAD_DIM
ATTN_V_WIDTH = N_HEADS * V_DIM
N_FOURIER_GROUPS = 4
FOURIER_GROUP_DIM = 64
FOURIER_WIDTH = N_FOURIER_GROUPS * FOURIER_GROUP_DIM
IN_WIDTH = 2 * ATTN_QK_WIDTH + ATTN_V_WIDTH + FOURIER_WIDTH + 2 * D_MODEL
N_EXPERTS = 16
CAPACITY_FACTOR = 2
D_FF = 2816
ROPE_THETA = 10000.0
Q_BLOCK = 128
EPS = 1e-6
SUBLN_EPS = 1e-5
N_MOD = 6

kernel_name = 'hybrid_diffusion_diffattn_fnet_ec'

def rmsnorm(x, g, eps=EPS):
    x32 = x.astype(jnp.float32)
    y = x32 * lax.rsqrt(jnp.mean(x32 * x32, axis=-1, keepdims=True) + eps)
    return (y * g.astype(jnp.float32)).astype(x.dtype)

def modulation(cond, w_mod, b_mod):
    m = jnp.einsum('...d,de->...e', jax.nn.silu(cond), w_mod) + b_mod
    m = m.reshape(m.shape[:-1] + (1, N_MOD, D_MODEL))
    return [m[..., i, :] for i in range(N_MOD)]

def rope_1d(x, pos):
    half = x.shape[-1] // 2
    freqs = ROPE_THETA ** (-jnp.arange(half, dtype=jnp.float32) / half)
    ang = pos.astype(jnp.float32)[:, None] * freqs
    cos, sin = jnp.cos(ang), jnp.sin(ang)
    x32 = x.astype(jnp.float32)
    x1, x2 = x32[..., :half], x32[..., half:]
    return jnp.concatenate([x1 * cos - x2 * sin, x1 * sin + x2 * cos], axis=-1).astype(x.dtype)

def axial_rope(x):
    S = x.shape[-2]
    rows = S // GRID_W
    row = jnp.repeat(jnp.arange(rows), GRID_W)
    col = jnp.tile(jnp.arange(GRID_W), rows)
    half = HEAD_DIM // 2
    return jnp.concatenate([rope_1d(x[..., :half], row), rope_1d(x[..., half:], col)], axis=-1)

def diff_attention(q, k, v, lam):
    B, H, _, Sq, DH = q.shape
    nb = Sq // Q_BLOCK
    scale = DH ** -0.5
    qb = q.reshape(B, H, 2, nb, Q_BLOCK, DH).transpose(3, 0, 1, 2, 4, 5)

    def block(qi):
        s = jnp.einsum('bhcqd,bhckd->bhcqk', qi, k).astype(jnp.float32) * scale
        p = jax.nn.softmax(s, axis=-1)
        a = p[:, :, 0] - lam * p[:, :, 1]
        return jnp.einsum('bhqk,bhkd->bhqd', a.astype(v.dtype), v)

    o = lax.map(block, qb)
    return o.transpose(1, 2, 0, 3, 4).reshape(B, H, Sq, v.shape[-1])

def token_mixer(h, w_in, lam, lam_init, g_subln, w_pa, w_pf, w_out, positional, ctx_k, ctx_v):
    B, S, _ = h.shape
    z = jnp.einsum('bsd,de->bse', h, w_in)
    splits = [ATTN_QK_WIDTH, 2 * ATTN_QK_WIDTH, 2 * ATTN_QK_WIDTH + ATTN_V_WIDTH,
              2 * ATTN_QK_WIDTH + ATTN_V_WIDTH + FOURIER_WIDTH,
              2 * ATTN_QK_WIDTH + ATTN_V_WIDTH + FOURIER_WIDTH + D_MODEL]
    q, k, v, f, ga, gf = jnp.split(z, splits, axis=-1)
    q = q.reshape(B, S, N_HEADS, 2, HEAD_DIM).transpose(0, 2, 3, 1, 4)
    k = k.reshape(B, S, N_HEADS, 2, HEAD_DIM).transpose(0, 2, 3, 1, 4)
    v = v.reshape(B, S, N_HEADS, V_DIM).transpose(0, 2, 1, 3)
    if positional:
        q = axial_rope(q)
        k = axial_rope(k)
    k_all, v_all = k, v
    if ctx_k is not None:
        k_all = jnp.concatenate([ctx_k, k], axis=3)
        v_all = jnp.concatenate([ctx_v, v], axis=2)
    o = diff_attention(q, k_all, v_all, lam)
    o = rmsnorm(o, g_subln, SUBLN_EPS) * (1.0 - lam_init)
    o = o.transpose(0, 2, 1, 3).reshape(B, S, ATTN_V_WIDTH)
    fg = f.reshape(B, S, N_FOURIER_GROUPS, FOURIER_GROUP_DIM).astype(jnp.float32)
    fm = jnp.fft.fft2(fg, axes=(1, 3), norm='ortho').real.astype(h.dtype).reshape(B, S, FOURIER_WIDTH)
    merged = jax.nn.sigmoid(ga) * jnp.einsum('bse,ed->bsd', o, w_pa) + \
        jax.nn.sigmoid(gf) * jnp.einsum('bse,ed->bsd', fm, w_pf)
    y = jnp.einsum('bsd,de->bse', merged, w_out)
    return y, k, v

def expert_choice_ffn(h, w_router, w_gate, w_up, w_down):
    B, S, D = h.shape
    T = B * S
    xt = h.reshape(T, D)
    aff = jax.nn.softmax(jnp.einsum('td,de->te', xt, w_router).astype(jnp.float32), axis=-1)
    cap = CAPACITY_FACTOR * T // N_EXPERTS
    g, idx = lax.top_k(aff.T, cap)
    xe = xt[idx]
    hid = jax.nn.silu(jnp.einsum('ecd,edf->ecf', xe, w_gate)) * jnp.einsum('ecd,edf->ecf', xe, w_up)
    ye = jnp.einsum('ecf,efd->ecd', hid, w_down) * g[..., None].astype(h.dtype)
    out = jnp.zeros_like(xt).at[idx.reshape(-1)].add(ye.reshape(-1, D))
    return out.reshape(B, S, D)

def layer(x, cond, lp, lam_init, positional, ctx_k, ctx_v):
    (w_mod, b_mod, g_pre_mix, g_post_mix, g_pre_ffn, g_post_ffn, w_in, lam_q1, lam_k1, lam_q2,
     lam_k2, g_subln, w_proj_attn, w_proj_fourier, w_out, w_router, w_gate, w_up, w_down) = lp
    sh1, sc1, gt1, sh2, sc2, gt2 = modulation(cond, w_mod, b_mod)
    lam = (jnp.exp(jnp.sum(lam_q1.astype(jnp.float32) * lam_k1.astype(jnp.float32)))
           - jnp.exp(jnp.sum(lam_q2.astype(jnp.float32) * lam_k2.astype(jnp.float32))) + lam_init)
    h = rmsnorm(x, g_pre_mix) * (1 + sc1) + sh1
    y, k, v = token_mixer(h, w_in, lam, lam_init, g_subln, w_proj_attn, w_proj_fourier, w_out,
                          positional, ctx_k, ctx_v)
    x = x + gt1 * rmsnorm(y, g_post_mix)
    h = rmsnorm(x, g_pre_ffn) * (1 + sc2) + sh2
    y = expert_choice_ffn(h, w_router, w_gate, w_up, w_down)
    x = x + gt2 * rmsnorm(y, g_post_ffn)
    return x, k, v

def setup_inputs(seed: int = 0) -> dict:
    key = jax.random.key(seed)
    ks = jax.random.split(key, 32)
    f32 = jnp.float32
    nrm = lambda k, shape, s: jax.random.normal(k, shape, f32) * s
    return {
        'x_prompt': nrm(ks[0], (BATCH, SEQ, D_MODEL), 1.0),
        'x_sample': nrm(ks[1], (DEC_BATCH, DEC_SEQ, D_MODEL), 1.0),
        'c': nrm(ks[2], (DEC_BATCH, D_MODEL), 1.0),
        'cache_k': nrm(ks[3], (DEC_BATCH, DEPTH, N_HEADS, PAST_LEN, 2 * HEAD_DIM), 1.0),
        'cache_v': nrm(ks[4], (DEC_BATCH, DEPTH, N_HEADS, PAST_LEN, V_DIM), 1.0),
        'c_ctx': nrm(ks[5], (D_MODEL,), 1.0),
        'w_mod': nrm(ks[6], (DEPTH, D_MODEL, N_MOD * D_MODEL), 0.5 * D_MODEL ** -0.5),
        'b_mod': nrm(ks[7], (DEPTH, N_MOD * D_MODEL), 0.02),
        'g_pre_mix': 1.0 + nrm(ks[8], (DEPTH, D_MODEL), 0.02),
        'g_post_mix': 1.0 + nrm(ks[9], (DEPTH, D_MODEL), 0.02),
        'g_pre_ffn': 1.0 + nrm(ks[10], (DEPTH, D_MODEL), 0.02),
        'g_post_ffn': 1.0 + nrm(ks[11], (DEPTH, D_MODEL), 0.02),
        'w_in': nrm(ks[12], (DEPTH, D_MODEL, IN_WIDTH), D_MODEL ** -0.5),
        'lam_q1': nrm(ks[13], (DEPTH, HEAD_DIM), 0.1),
        'lam_k1': nrm(ks[14], (DEPTH, HEAD_DIM), 0.1),
        'lam_q2': nrm(ks[15], (DEPTH, HEAD_DIM), 0.1),
        'lam_k2': nrm(ks[16], (DEPTH, HEAD_DIM), 0.1),
        'g_subln': 1.0 + nrm(ks[17], (DEPTH, V_DIM), 0.02),
        'w_proj_attn': nrm(ks[18], (DEPTH, ATTN_V_WIDTH, D_MODEL), ATTN_V_WIDTH ** -0.5),
        'w_proj_fourier': nrm(ks[19], (DEPTH, FOURIER_WIDTH, D_MODEL), FOURIER_WIDTH ** -0.5),
        'w_out': nrm(ks[20], (DEPTH, D_MODEL, D_MODEL), D_MODEL ** -0.5),
        'w_router': nrm(ks[21], (DEPTH, D_MODEL, N_EXPERTS), D_MODEL ** -0.5),
        'w_gate': nrm(ks[22], (DEPTH, N_EXPERTS, D_MODEL, D_FF), D_MODEL ** -0.5),
        'w_up': nrm(ks[23], (DEPTH, N_EXPERTS, D_MODEL, D_FF), D_MODEL ** -0.5),
        'w_down': nrm(ks[24], (DEPTH, N_EXPERTS, D_FF, D_MODEL), D_FF ** -0.5),
    }

def reference(x_prompt, x_sample, c, cache_k, cache_v, c_ctx, w_mod, b_mod, g_pre_mix, g_post_mix,
              g_pre_ffn, g_post_ffn, w_in, lam_q1, lam_k1, lam_q2, lam_k2, g_subln, w_proj_attn,
              w_proj_fourier, w_out, w_router, w_gate, w_up, w_down):
    xp, xs = x_prompt, x_sample
    new_k, new_v = [], []
    for l in range(DEPTH):
        lam_init = 0.8 - 0.6 * math.exp(-0.3 * l)
        lp = (w_mod[l], b_mod[l], g_pre_mix[l], g_post_mix[l], g_pre_ffn[l], g_post_ffn[l], w_in[l],
              lam_q1[l], lam_k1[l], lam_q2[l], lam_k2[l], g_subln[l], w_proj_attn[l],
              w_proj_fourier[l], w_out[l], w_router[l], w_gate[l], w_up[l], w_down[l])
        xp, kp, vp = layer(xp, c_ctx, lp, lam_init, False, None, None)
        Bp, H, _, Sp, DH = kp.shape
        new_k.append(kp.transpose(0, 1, 3, 2, 4).reshape(Bp, H, Sp, 2 * DH))
        new_v.append(vp)
        ck = cache_k[:, l]
        Bd, _, L, _ = ck.shape
        ck = ck.reshape(Bd, N_HEADS, L, 2, HEAD_DIM).transpose(0, 1, 3, 2, 4)
        xs, _, _ = layer(xs, c, lp, lam_init, True, ck, cache_v[:, l])
    new_cache_k = jnp.stack(new_k, axis=1)
    new_cache_v = jnp.stack(new_v, axis=1)
    return (xp, xs, new_cache_k, new_cache_v)


_drawn_inputs = setup_inputs


def setup_inputs(seed=0):
    import zlib

    import numpy as np

    out = dict(_drawn_inputs(seed))
    spreads = {}
    factors = {'g_post_ffn': 8.0, 'lam_k1': 2.902, 'lam_k2': 2.874, 'g_subln': 3.295}
    for name, (base, spread) in spreads.items():
        noise = np.random.default_rng([zlib.crc32(name.encode()), seed]).standard_normal(out[name].shape)
        drawn = base * np.exp(spread * noise) if base else spread * noise
        out[name] = __import__('jax').numpy.asarray(drawn.astype(out[name].dtype))
    for name, factor in factors.items():
        out[name] = (out[name] * factor).astype(out[name].dtype)
    return out
```

```python
from contextlib import ExitStack
import math

import numpy as np
import concourse.bass as bass
from concourse import mybir

F32 = mybir.dt.float32
F32R = mybir.dt.float32r
U32 = mybir.dt.uint32
I32 = mybir.dt.int32
ALU = mybir.AluOpType
ACT = mybir.ActivationFunctionType
AXX = mybir.AxisListType.X

P = 128
D = 1024
KD = D // P
LAT = 512
CTX = 128
TOK = LAT + CTX
NT = TOK // P
NL = LAT // P
H = 6
DH = 64
QKV = H * 2 * DH
HALF = QKV // 2
FW = 256
FD = 64
KEYS = P + LAT + CTX
E_ = 16
FF = 2816
NF = FF // P
NS = NF // 2
CL = 2 * LAT // E_
CC = 2 * CTX // E_
CT = CL + CC
NMOD = 6
GRID_W = 64
LAM_INIT = 0.8 - 0.6 * math.exp(-0.3 * 0)
EPS = 1e-6
SUB_EPS = 1e-5
GUR = 11
DR = 11
WB = 3
NITEM = H * NT

SB0 = 16512


def constants():
    tok = np.arange(LAT)
    half = DH // 4
    fr = 10000.0 ** (-np.arange(half) / half)
    ang = np.stack([np.outer(tok // GRID_W, fr), np.outer(tok % GRID_W, fr)], 1)
    cos = np.repeat(np.cos(ang)[:, :, None, :], 2, 2)
    sin = np.stack([-np.sin(ang), np.sin(ang)], 2)
    rope = np.stack([cos.reshape(LAT, DH), sin.reshape(LAT, DH)], 1)

    def dft(n):
        a = 2 * np.pi * (np.outer(np.arange(n), np.arange(n)) % n) / n
        return np.cos(a), np.sin(a)

    def seq(n):
        c, s = dft(n)
        return np.stack([c, s], 1) / math.sqrt(n * FD)

    c, s = dft(FD)
    chan = np.concatenate([np.kron(np.eye(2), c), np.kron(np.eye(2), -s)], 1)
    return {"rope": rope, "dftl": seq(LAT), "dftc": seq(CTX), "chan": chan, "eye": np.eye(P)}


def program(nc, a, o):
    w_mod, w_in, w_out = a["w_mod"][0], a["w_in"][0], a["w_out"][0]
    w_gate, w_up, w_down = a["w_gate"][0], a["w_up"][0], a["w_down"][0]
    y_prompt, y_sample, new_k, new_v = o

    with ExitStack() as ctx:
        def at(name, off, shape, dt=F32):
            return nc.alloc_sbuf_tensor_at(name, shape, dt, offset=SB0 + off)

        def sem(name):
            return ctx.enter_context(nc.semaphore(name))

        ps = ctx.enter_context(nc.psum_tensor("ps", [P, 8, 512], F32))
        xn_dram = nc.dram_tensor("xn_dram", [TOK, D], F32)
        ysum_dram = nc.dram_tensor("ysum_dram", [TOK, D], F32)

        gu_ring = at("gu_ring", 0, [P, GUR, KD, 256])
        D0 = GUR * 8192
        d_ring = [at(f"d_ring{i}", D0 + i * 4096, [P, D]) for i in range(DR)]
        RING = D0 + DR * 4096
        x1 = at("x1", RING, [P, NT, D])
        E0 = RING + NT * D * 4
        zero = at("zero", 0, [P, D])
        lamv = at("lamv", 4096, [P, 4, DH])
        qT = at("qT", 0, [P, H, TOK])
        kT = at("kT", 15360, [P, H, KEYS])
        vr = at("vr", 33792, [P, 6, QKV])
        xn = at("xn", 52224, [P, NT, D])
        oT = at("oT", 52224, [P, H, TOK])
        fmT = at("fmT", 67584, [P, 2, TOK])
        hT = at("hT", 72704, [P, KD, TOK])
        fT = at("fT", 93184, [P, 2, TOK])
        Gs = at("Gs", 98304, [P, NT, 2, 256])
        dftl = at("dftl", 108544, [P, NL, 2, LAT])
        dftc = at("dftc", 124928, [P, 2, CTX])
        chan = at("chan", 125952, [P, 256])
        w_pa = at("w_pa", 93184, [P, H, D])
        w_pf = at("w_pf", 117760, [P, 2, D])
        rope = at("rope", 126976, [P, NL, 2, DH])
        zr = [at(f"zr{i}", 129024 + i * 1536, [P, HALF]) for i in range(3)]
        zt = at("zt", 133632, [P, HALF])
        gate_w = [at("gate_w0", E0, [P, 2, KD, 256])] + [
            at(f"gate_w{i}", (i - 1) * 16384, [P, 2, KD, 256]) for i in range(1, 4)]
        sg_a = at("sg_a", 126976, [P, TOK])
        sg_f = at("sg_f", 129536, [P, TOK])
        t_pa = at("t_pa", 132096, [P, TOK])
        B0 = D0 + 5 * 4096
        ggrow = at("ggrow", B0, [P, 2, D])
        row = [at(f"row{i}", B0 + 8192 + i * 4096, [P, D]) for i in range(2)]
        h2T = [at(f"h2T{i}", B0 + 16384 + i * 4096, [P, KD, P]) for i in range(2)]
        fin = at("fin", 0, [P, NT, D])
        fout = at("fout", 20480, [P, NT, D])
        ggrow2 = at("ggrow2", 40960, [P, 2, D])
        slab = [at(f"slab{i}", E0 + i * 16384, [P, KD, 512]) for i in range(3)]
        prow = at("prow", E0 + 49152, [97, P])
        ck_rows = at("ck_rows", E0 + 49152 + 512, [P, QKV])
        wo_sb = at("wo_sb", E0, [P, KD, D])
        M0 = E0 + 32768
        mT = at("mT", M0, [P, KD, TOK])
        pr = [at(f"pr{i}", 126976 + i * 2560, [P, TOK]) for i in range(3)] + [at("pr3", M0, [P, TOK])]
        am = [at(f"am{i}", M0 + 2560 * (1 + i), [P, TOK]) for i in range(2)]
        aT = [at(f"aT{i}", M0 + 2560 * (3 + i), [P, TOK]) for i in range(2)]
        on = [at(f"on{i}", M0 + 12800 + 512 * i, [P, P]) for i in range(2)]
        ojunk = at("ojunk", M0 + 13824, [P, P])
        orow = [at(f"orow{i}", M0 + 16384 + 512 * i, [P, P]) for i in range(3)]
        negm = at("negm", M0 + 14336, [P, 2 * NITEM])
        psumr = at("psumr", M0 + 14592, [P, 2 * NITEM])
        rs = at("rs", M0 + 14848, [P, 2 * NITEM])
        nl = at("nl", M0 + 15104, [P, NITEM])
        oss = at("oss", M0 + 15360, [P, NITEM])
        ort = at("ort", M0 + 15616, [P, NITEM])
        xe = at("xe", E0, [CT, D])
        yr = at("yr", E0 + 4096, [CT, D])
        xeT = at("xeT", E0 + 8192, [P, KD, CT])
        sil = [at(f"sil{i}", E0 + 10752 + 1024 * i, [CT, 256]) for i in range(2)]
        hid = [at(f"hid{i}", E0 + 12800 + 1024 * i, [CT, 256]) for i in range(2)]
        x_hi = at("x_hi", E0 + 14848, [P, KD, CT], F32R)
        x_lo = at("x_lo", E0 + 17408, [P, KD, CT], F32R)
        h_hi = [at(f"h_hi{i}", E0 + 19968 + 640 * i, [P, 2, CT], F32R) for i in range(2)]
        h_lo = [at(f"h_lo{i}", E0 + 21248 + 640 * i, [P, 2, CT], F32R) for i in range(2)]
        w_hi = at("w_hi", E0 + 22528, [P, WB, 2, 512], F32R)
        w_lo = at("w_lo", E0 + 22528 + WB * 4096, [P, WB, 2, 512], F32R)
        work = at("work", E0 + 22528, [E_, LAT])
        topv = at("topv", E0 + 24576, [E_, CT])
        topi = at("topi", E0 + 24896, [E_, CT], U32)
        topf = at("topf", E0 + 25216, [E_, CT])
        S0 = [E0 + 53248]

        def small(name, shape, dt=F32):
            off = S0[0]
            S0[0] += (int(np.prod(shape[1:])) * 4 + 31) // 32 * 32
            return at(name, off, shape, dt)

        ident = small("ident", [P, P])
        w_r = small("w_r", [P, KD, E_])
        pT = small("pT", [P, 97])
        sil_c = small("sil_c", [P, 2, KD])
        modT = small("modT", [P, NMOD * KD, 2])
        A1, A2 = small("A1", [P, 2, KD]), small("A2", [P, 2, KD])
        GG1, GG2 = small("GG1", [P, 2, KD]), small("GG2", [P, 2, KD])
        mhalf = small("mhalf", [P, 1])
        gsub = small("gsub", [P, 1])
        ssx, rsx = small("ssx", [P, NT]), small("rsx", [P, NT])
        ssy, rsy = small("ssy", [P, NT]), small("rsy", [P, NT])
        ss2, rs2 = small("ss2", [P, NT]), small("rs2", [P, NT])
        lsum, lexp, nlam = small("lsum", [P, 2]), small("lexp", [P, 2]), small("nlam", [P, 1])
        lneg, lden, lrec = small("lneg", [P, NT]), small("lden", [P, NT]), small("lrec", [P, NT])
        aff = [small(f"aff{i}", [P, E_]) for i in range(2)]
        work_c = small("work_c", [E_, CTX])
        idxT = small("idxT", [CT, E_], I32)
        gT = small("gT", [CT, E_])
        idx_g, idx_s = small("idx_g", [CT, 1], I32), small("idx_s", [CT, 1], I32)
        assert SB0 + S0[0] <= 229344, S0[0]

        G_PRE_MIX, G_POST_MIX, G_PRE_FFN, G_POST_FFN, C_COL = 48, 56, 64, 72, 80
        SH1, SC1, GT1, SH2, SC2, GT2 = (KD * i for i in range(NMOD))

        ld_eye, ld_par, ld_lam, ld_tab, ld_cache, ld_dft, ld_wr, ld_wp, ld_wo = (
            sem(n) for n in ("ld_eye", "ld_par", "ld_lam", "ld_tab", "ld_cache", "ld_dft", "ld_wr", "ld_wp", "ld_wo"))
        ld_x = [sem(f"ld_x{t}") for t in range(NT)]
        ld_slab = [sem(f"ld_slab{i}") for i in range(3)]
        ld_gate = [sem(f"ld_gate{i}") for i in range(4)]
        par_T, par_ready, silu_ready = sem("par_T"), sem("par_ready"), sem("silu_ready")
        x_sq, xn_ready = sem("x_sq"), sem("xn_ready")
        lam_sum, lam_exp, lam_ready = sem("lam_sum"), sem("lam_exp"), sem("lam_ready")
        zero_set = sem("zero_set")
        xT_lat, xT_ctx = sem("xT_lat"), sem("xT_ctx")
        mod_done, mod1_ready, mod2_ready = sem("mod_done"), sem("mod1_ready"), sem("mod2_ready")
        h_even, h_odd = sem("h_even"), sem("h_odd")
        z_done, z_act, z_dve = sem("z_done"), sem("z_act"), sem("z_dve")
        t_done, t_ev = sem("t_done"), sem("t_ev")
        nk_stored, nv_stored = sem("nk_stored"), sem("nv_stored")
        g_done, g_ev, fm_done, fm_ev = sem("g_done"), sem("g_ev"), sem("fm_done"), sem("fm_ev")
        s_done, negm_ready, p_ready, a_ready = sem("s_done"), sem("negm_ready"), sem("p_ready"), sem("a_ready")
        aT_done, aT_ev, pv_done, o_sq, on_ready, oT_done, oT_ev = (
            sem(n) for n in ("aT_done", "aT_ev", "pv_done", "o_sq", "on_ready", "oT_done", "oT_ev"))
        mg_done, sig_done, mg_ev = sem("mg_done"), sem("sig_done"), sem("mg_ev")
        gg_done, gg_ev = sem("gg_done"), sem("gg_ev")
        y_done, y_sq, y_used, x1_ready, x1_sq, x2_ready, x2_T = (
            sem(n) for n in ("y_done", "y_sq", "y_used", "x1_ready", "x1_sq", "x2_ready", "x2_T"))
        h2_a, h2_v, lg_done, lneg_ready, lexp_ready, aff_ready, affT_done, affT_used = (
            sem(n) for n in ("h2_a", "h2_v", "lg_done", "lneg_ready", "lexp_ready", "aff_ready", "affT_done", "affT_used"))
        x2_stored = [sem(f"x2_stored{i}") for i in range(2)]
        top_ready, topT_done, idx_ready = sem("top_ready"), sem("topT_done"), sem("idx_ready")
        w_hi_ready, w_lo_ready, w_used = sem("w_hi_ready"), sem("w_lo_ready"), sem("w_used")
        x_hi_ready = sem("x_hi_ready")
        hT_hi_ready, hT_lo_ready = sem("hT_hi_ready"), sem("hT_lo_ready")
        mixer_gone, router_gone = sem("mixer_gone"), sem("router_gone")
        gu_ld = [sem(f"gu_ld{i}") for i in range(GUR)]
        d_ld = [sem(f"d_ld{i}") for i in range(DR)]
        idxg_set, idxs_set, gathered, scattered = (
            sem(n) for n in ("idxg_set", "idxs_set", "gathered", "scattered"))
        pool_turn = sem("pool_turn")
        xeT_done, xeT_ev, sil_ready, hid_ready, hidT_done, yr_ready = (
            sem(n) for n in ("xeT_done", "xeT_ev", "sil_ready", "hid_ready", "hidT_done", "yr_ready"))
        ld_fin = [sem(f"ld_fin{t}") for t in range(NT)]
        gg2_done, gg2_ev, f_sq, f_ready, out_stored = (
            sem(n) for n in ("gg2_done", "gg2_ev", "f_sq", "f_ready", "out_stored"))
        o_rows = sem("o_rows")
        x_rs, o_rs, y_rs, x1_rs, f_rs = (sem(n) for n in ("x_rs", "o_rs", "y_rs", "x1_rs", "f_rs"))
        p_chain = sem("p_chain")
        v_chain, v_loop = sem("v_chain"), sem("v_loop")

        MOD1 = [(w_mod, 512 * i, 512) for i in range(4)]
        MOD2 = [(w_mod, 512 * i, 512) for i in range(4, 12)]
        INP = [(w_in, 3 * QKV, FW), (w_in, QKV, HALF), (w_in, QKV + HALF, HALF), (w_in, 0, HALF), (w_in, HALF, HALF),
               (w_in, 2 * QKV, HALF), (w_in, 2 * QKV + HALF, HALF)]
        SLABS = MOD1 + INP + MOD2
        N_IN, N_MOD2 = len(MOD1), len(MOD1) + len(INP)

        UNITS = [("f", N_IN, c, t) for c in range(2) for t in (0, NL)]
        for n, kind in enumerate("kkqqvv"):
            UNITS += [(kind, N_IN + 1 + n, n % 2, t) for t in range(NT)]
        ev_of, counts = [], {"a": 0, "v": 0}
        for kind, _, _, t in UNITS:
            who = "v" if kind in "qk" and t < NL else "a"
            counts[who] += 1
            ev_of.append((who, counts[who]))
        QK = [u for u, x in enumerate(UNITS) if x[0] in "qk"]
        NTR = len(QK) + 2

        def wait_unit(eng, u):
            who, n = ev_of[u]
            eng.wait_ge(z_act if who == "a" else z_dve, n)

        items = [(h, t) for h in range(H) for t in range(NT)]
        TILES = [NL] + list(range(NL))

        def cond(t):
            return 1 if t == NL else 0

        def slab_multiplied(eng, n):
            if N_IN <= n < N_MOD2:
                eng.wait_ge(z_done, max(u for u, x in enumerate(UNITS) if x[1] == n) + 1)
            else:
                eng.wait_ge(mod_done, n + 1 if n < N_IN else n + 1 - len(INP))

        def pair(s):
            a_, b_ = (2 * s) % GUR, (2 * s + 1) % GUR
            return min(a_, b_), max(a_, b_)

        STEPS = []
        for s_ in range(NS + 2):
            STEPS.append(([("gu", s_, q) for q in range(KD // 2)] if s_ < NS else []) +
                         ([("d", s_ - 2, f) for f in range(2)] if s_ >= 2 else []))
        WUNITS = [x for y in STEPS for x in y]
        NW = len(WUNITS)
        gu_end = [max(n for n, x in enumerate(WUNITS) if x[:2] == ("gu", s_)) + 1 for s_ in range(NS)]
        d_end = [max(n for n, x in enumerate(WUNITS) if x[:2] == ("d", s_)) + 1 for s_ in range(NS)]
        assert NW % WB == 0

        def unit_src(unit):
            kind, s, q = unit
            if kind == "d":
                return d_ring[(2 * s + q) % DR][:, :].rearrange("p (a n) -> p a n", a=2)
            lo, hi = pair(s)
            return gu_ring[:, lo:hi + 1:hi - lo, 2 * q:2 * q + 2, :]

        def unit_dst(buf, unit, n):
            dst = buf[:, n % WB, :, :]
            if unit[0] == "gu":
                return dst.rearrange("p k (g n) -> p g k n", g=2)
            return dst

        def gate_cols(s):
            first = (2 * s) % GUR == pair(s)[0]
            return (slice(0, 256), slice(256, 512)) if first else (slice(256, 512), slice(0, 256))

        def loaded(eng, n):
            eng.wait_ge(ld_slab[n % 3], 16 * (n // 3 + 1))

        block = ctx.enter_context(nc.Block())

        @block.sync
        def _(sp):
            sp.dma_start(ident[:, :], a["eye"]).then_inc(ld_eye, 16)
            for t in TILES:
                src = a["x_prompt"][0] if t == NL else a["x_sample"][0, t * P:(t + 1) * P]
                sp.dma_start(x1[:, t, :], src).then_inc(ld_x[t], 16)
            par = [(a["b_mod"], 0, 48), (a["g_pre_mix"], 48, 8), (a["g_post_mix"], 56, 8), (a["g_pre_ffn"], 64, 8),
                   (a["g_post_ffn"], 72, 8), (a["c"], 80, 8)]
            for v, r, n in par:
                sp.dma_start(prow[r:r + n, :], v.rearrange("o (k p) -> (o k) p", p=P)).then_inc(ld_par, 16)
            sp.dma_start(prow[88:96, :], a["c_ctx"].rearrange("(k p) -> k p", p=P)).then_inc(ld_par, 16)
            sp.dma_start(prow[96:97, :], a["g_subln"]).then_inc(ld_par, 16)

            def load_slab(n):
                w, c0, cols = SLABS[n]
                if n >= 3:
                    slab_multiplied(sp, n - 3)
                sp.dma_start(slab[n % 3][:, :, 0:cols],
                             w[:, c0:c0 + cols].rearrange("(k p) n -> p k n", p=P)).then_inc(ld_slab[n % 3], 16)

            for n in range(3):
                load_slab(n)
            for i, name in enumerate(("lam_q1", "lam_k1", "lam_q2", "lam_k2")):
                sp.dma_start(lamv[:, i, :], a[name].to_broadcast([P, DH])).then_inc(ld_lam, 16)
            sp.dma_start(rope[:, :, :, :], a["rope"].rearrange("(t p) c d -> p t c d", p=P)).then_inc(ld_tab, 16)
            sp.dma_start(w_r[:, :, :], a["w_router"][0].rearrange("(k p) e -> p k e", p=P)).then_inc(ld_wr, 16)
            sp.dma_start(ck_rows[:, :].rearrange("p (h d) -> p h d", h=H),
                         a["cache_k"][0, 0].rearrange("h s d -> s h d")).then_inc(ld_cache, 16)
            sp.dma_start(vr[:, 0, :].rearrange("p (h d) -> p h d", h=H),
                         a["cache_v"][0, 0].rearrange("h s d -> s h d")).then_inc(ld_cache, 16)
            sp.dma_start(dftl[:, :, :, :], a["dftl"].rearrange("(t p) c n -> p t c n", p=P)).then_inc(ld_dft, 16)
            sp.dma_start(dftc[:, :, :], a["dftc"]).then_inc(ld_dft, 16)
            sp.dma_start(chan[:, :], a["chan"]).then_inc(ld_dft, 16)
            for n in range(3, len(SLABS)):
                load_slab(n)
            sp.wait_ge(fm_done, 4)
            sp.dma_start(w_pa[:, :, :], a["w_proj_attn"][0].rearrange("(h p) n -> p h n", p=P)).then_inc(ld_wp, 16)
            sp.dma_start(w_pf[:, :, :], a["w_proj_fourier"][0].rearrange("(h p) n -> p h n", p=P)).then_inc(ld_wp, 16)
            for j in range(4):
                if j == 0:
                    slab_multiplied(sp, len(SLABS) - 1)
                if j == 1:
                    sp.wait_ge(pv_done, NITEM)
                for g in range(2):
                    c0 = 3 * QKV + FW + g * D + j * 256
                    sp.dma_start(gate_w[j][:, g, :, :],
                                 w_in[:, c0:c0 + 256].rearrange("(k p) n -> p k n", p=P)).then_inc(ld_gate[j], 16)
            sp.wait_ge(mg_done, 8)
            sp.dma_start(wo_sb[:, :, :], w_out.rearrange("(k p) n -> p k n", p=P)).then_inc(ld_wo, 16)

            def load_expert(e, turn):
                for s in range(NS):
                    for kind, j in (("gu", 2 * s), ("gu", 2 * s + 1), ("d", 2 * s), ("d", 2 * s + 1)):
                        ends = gu_end if kind == "gu" else d_end
                        if j >= GUR:
                            n = ends[(j - GUR) // 2]
                            sp.wait_ge(w_lo_ready, n if turn is None else turn * NW + (NW + n))
                        elif turn is None:
                            sp.wait_ge(router_gone if kind == "d" and j >= 5 else mixer_gone, 1)
                        else:
                            sp.wait_ge(w_lo_ready, turn * NW + ends[(j + GUR) // 2])
                        if kind == "gu":
                            w = (w_gate, w_up)[j % 2]
                            src = w[bass.ds(e, 1), :, s * 256:(s + 1) * 256].rearrange("o (k p) n -> p (o k) n", p=P)
                            sp.dma_start(gu_ring[:, j % GUR, :, :], src).then_inc(gu_ld[j % GUR], 16)
                        else:
                            src = w_down[bass.ds(e, 1), j * P:(j + 1) * P, :].rearrange("o p n -> p (o n)")
                            sp.dma_start(d_ring[j % DR][:, :], src).then_inc(d_ld[j % DR], 16)

            load_expert(0, None)
            with sp.Fori(0, E_ - 1) as turn:
                load_expert(turn + 1, turn)
            sp.wait_ge(scattered, 16 * (NT + E_))
            for t in range(NT):
                sp.dma_start(fin[:, t, :], ysum_dram[t * P:(t + 1) * P, :]).then_inc(ld_fin[t], 16)
            for t in range(NT):
                sp.wait_ge(f_ready, t + 1)
                dst = y_prompt[0] if t == NL else y_sample[0, t * P:(t + 1) * P]
                sp.dma_start(dst, fout[:, t, :]).then_inc(out_stored, 16)
            sp.wait_ge(out_stored, 16 * NT)
            sp.wait_ge(nk_stored, 32)
            sp.wait_ge(nv_stored, 16)

        @block.gpsimd
        def _(pool):
            steps = [0]

            def link(ins):
                steps[0] += 1
                ins.then_inc(p_chain, 1)
                pool.wait_ge(p_chain, steps[0])

            def rstd(out, ss, n, eps):
                link(pool.tensor_scalar(out, ss, 1.0 / n, eps, ALU.mult, ALU.add))
                return pool.tensor_tensor(out, out, mhalf[:, :], ALU.pow)

            pool.memset(mhalf[:, :], -0.5).then_inc(zero_set, 1)
            pool.memset(zero[:, :], 0.0).then_inc(zero_set, 1)
            pool.wait_ge(zero_set, 2)
            for i, t in enumerate(TILES):
                pool.wait_ge(x_sq, i + 1)
                rstd(rsx[:, t:t + 1], ssx[:, t:t + 1], D, EPS).then_inc(x_rs, 1)
            for t in range(NT):
                pool.dma_start(ysum_dram[t * P:(t + 1) * P, :], zero[:, :]).then_inc(scattered, 16)
            for n in range(2):
                u = QK[NT * n + NL]
                wait_unit(pool, u)
                pool.dma_start(new_k[0, 0, 3 * n:3 * n + 3].rearrange("h s d -> s h d"),
                               zr[(NT * n + NL) % 3][:, :].rearrange("p (h d) -> p h d", h=3)).then_inc(nk_stored, 16)
            wait_unit(pool, len(UNITS) - 1)
            pool.dma_start(new_v[0, 0].rearrange("h s d -> s h d"),
                           vr[:, 5, :].rearrange("p (h d) -> p h d", h=H)).then_inc(nv_stored, 16)
            for i in range(NITEM):
                pool.wait_ge(o_sq, i + 1)
                rstd(ort[:, i:i + 1], oss[:, i:i + 1], 2 * DH, SUB_EPS).then_inc(o_rs, 1)
            for i, t in enumerate(TILES):
                pool.wait_ge(y_sq, i + 1)
                rstd(rsy[:, i:i + 1], ssy[:, i:i + 1], D, EPS).then_inc(y_rs, 1)
                pool.wait_ge(x1_sq, i + 1)
                rstd(rs2[:, i:i + 1], ss2[:, i:i + 1], D, EPS).then_inc(x1_rs, 1)
                pool.wait_ge(x2_ready, i + 1)
                pool.dma_start(xn_dram[t * P:(t + 1) * P, :], row[i % 2][:, :]).then_inc(x2_stored[i % 2], 16)
            pool.wait_ge(x2_stored[0], 16 * ((NT + 1) // 2))
            pool.wait_ge(x2_stored[1], 16 * (NT // 2))
            pool.wait_ge(idx_ready, 1)
            pool.sem_inc(router_gone, 1)

            def gather():
                pool.indirect_dma_start(xe[:, :], None, xn_dram[:, :],
                                        bass.IndirectOffsetOnAxis(ap=idx_g[:, :], axis=0)).then_inc(gathered, 16)

            def scatter():
                pool.indirect_dma_start(ysum_dram[:, :], bass.IndirectOffsetOnAxis(ap=idx_s[:, :], axis=0),
                                        yr[:, :], None, compute_op=ALU.add).then_inc(scattered, 16)

            pool.tensor_copy(idx_g[:, :], idxT[:, 0:1]).then_inc(idxg_set, 1)
            pool.wait_ge(idxg_set, 1)
            gather()
            with pool.Fori(0, E_ - 1) as e:
                pool.wait_ge(xeT_done, e + 1)
                pool.sem_inc(pool_turn, 1)
                pool.tensor_copy(idx_g[:, :], idxT[:, bass.ds(e + 1, 1)]).then_inc(idxg_set, 1)
                pool.wait_ge(idxg_set, e + 2)
                pool.sem_inc(pool_turn, 1)
                gather()
                pool.wait_ge(scattered, (e + NT) * 16)
                pool.sem_inc(pool_turn, 1)
                pool.tensor_copy(idx_s[:, :], idxT[:, bass.ds(e, 1)]).then_inc(idxs_set, 1)
                pool.wait_ge(idxs_set, e + 1)
                pool.sem_inc(pool_turn, 1)
                pool.wait_ge(yr_ready, e + 2)
                pool.sem_inc(pool_turn, 1)
                scatter()
            pool.wait_ge(scattered, 16 * (E_ - 1 + NT))
            pool.tensor_copy(idx_s[:, :], idxT[:, E_ - 1:E_]).then_inc(idxs_set, 1)
            pool.wait_ge(idxs_set, E_)
            pool.wait_ge(yr_ready, E_ + 1)
            scatter()
            pool.wait_ge(scattered, 16 * (NT + E_))
            for t in range(NT):
                pool.wait_ge(f_sq, t + 1)
                rstd(rsx[:, t:t + 1], ssx[:, t:t + 1], D, EPS).then_inc(f_rs, 1)

        @block.tensor
        def _(pe):
            def mm(out, lhsT, rhs, first, last, **kw):
                return pe.matmul(out, lhsT, rhs, start=first, stop=last, **kw)

            pe.wait_ge(ld_eye, 16)
            pe.wait_ge(ld_par, 16 * 8)
            pe.transpose(ps[:, 7, 384:384 + 97], prow[:, :], ident[0:97, 0:97]).then_inc(par_T, 1)

            def x_lat(k):
                for t in range(NL):
                    last = pe.transpose(ps[:, k % 4, t * P:(t + 1) * P], xn[:, t, k * P:(k + 1) * P], ident[:, :])
                last.then_inc(xT_lat, 1)

            pe.wait_ge(xn_ready, NT)
            for k in range(4):
                x_lat(k)
            for k in range(KD):
                last = pe.transpose(ps[:, 4 + k // 4, (k % 4) * P:(k % 4 + 1) * P], xn[:, NL, k * P:(k + 1) * P],
                                    ident[:, :])
            last.then_inc(xT_ctx, 1)

            def modulation(n, m0):
                loaded(pe, n)
                for m in range(4):
                    for k in range(KD):
                        c = 256 + 2 * (m0 + m)
                        last = mm(ps[:, 7, c:c + 2], slab[n % 3][:, k, m * P:(m + 1) * P], sil_c[:, :, k],
                                  k == 0, k == KD - 1)
                last.then_inc(mod_done, 1)

            pe.wait_ge(silu_ready, 1)
            for n in range(4):
                modulation(n, 4 * n)
            for k in range(4, KD):
                pe.wait_ge(h_even if k % 2 == 0 else h_odd, (k - 4) // 2 + 2)
                x_lat(k)

            pe.wait_ge(h_even, KD // 2 + 1)
            pe.wait_ge(h_odd, KD // 2 + 1)

            def transposes(j):
                b = ps[:, 4 + j % 2, 0:HALF]
                if j >= 2:
                    pe.wait_ge(t_ev, j - 1)
                if j < len(QK):
                    wait_unit(pe, QK[j])
                    src = zr[j % 3][:, :]
                else:
                    pe.wait_ge(ld_cache, 32)
                    src = ck_rows[:, (j - len(QK)) * HALF:(j - len(QK) + 1) * HALF]
                for h in range(3):
                    last = pe.transpose(b[:, h * P:(h + 1) * P], src[:, h * P:(h + 1) * P], ident[:, :])
                last.then_inc(t_done, 1)

            for u, (kind, n, half, t) in enumerate(UNITS):
                if u == 0 or UNITS[u - 1][1] != n:
                    loaded(pe, n)
                if u >= 4:
                    wait_unit(pe, u - 4)
                for k in range(KD):
                    if kind == "f":
                        c0, c1 = (0, LAT) if t < NL else (LAT, TOK)
                        last = mm(ps[:, u % 4, 0:c1 - c0], slab[n % 3][:, k, half * P:(half + 1) * P],
                                  hT[:, k, c0:c1], k == 0, k == KD - 1)
                    else:
                        last = mm(ps[:, u % 4, 0:HALF], hT[:, k, t * P:(t + 1) * P], slab[n % 3][:, k, 0:HALF],
                                  k == 0, k == KD - 1)
                last.then_inc(z_done, 1)
                if u - 1 in QK:
                    transposes(QK.index(u - 1))
            for j in range(len(QK), NTR):
                transposes(j)
            for i in range(8):
                modulation(N_MOD2 + i, 16 + 4 * i)

            pe.wait_ge(ld_dft, 48)
            wait_unit(pe, 3)
            pe.wait_ge(t_ev, NTR)
            g = 0
            for t in range(NT):
                for c in range(2):
                    if g >= 3:
                        pe.wait_ge(g_ev, g - 2)
                    mm(ps[:, 4 + g % 3, 0:256], fT[:, c, t * P:(t + 1) * P], chan[:, :], True, True).then_inc(g_done, 1)
                    g += 1
            pe.wait_ge(g_ev, 2 * NT)
            wait_unit(pe, len(UNITS) - 1)
            for c in range(2):
                for i in range(2 * NL):
                    t, part = divmod(i, 2)
                    last = mm(ps[:, c, :], Gs[:, t, c, part * P:(part + 1) * P], dftl[:, t, part, :], i == 0,
                              i == 2 * NL - 1)
                last.then_inc(fm_done, 1)
            for c in range(2):
                for part in range(2):
                    last = mm(ps[:, 2 + c, 0:CTX], Gs[:, NL, c, part * P:(part + 1) * P], dftc[:, part, :], part == 0,
                              part == 1)
                last.then_inc(fm_done, 1)

            pe.wait_ge(fm_ev, 4)
            pe.wait_ge(mod2_ready, 1)

            def keys(t):
                return (P + LAT, KEYS) if t == NL else (0, P + LAT)

            def scores(i):
                h, t = items[i]
                k0, k1 = keys(t)
                for c in range(2):
                    n = 2 * i + c
                    if n >= 2:
                        pe.wait_ge(p_ready, n - 1)
                    b = 2 * (n % 2)
                    q = qT[DH * c:DH * (c + 1), h, t * P:(t + 1) * P]
                    for j, x0 in enumerate(range(k0, k1, 512)):
                        x1_ = min(x0 + 512, k1)
                        last = mm(ps[:, b + j, 0:x1_ - x0], q, kT[DH * c:DH * (c + 1), h, x0:x1_], True, True)
                    last.then_inc(s_done, 1)

            def trans_a(i):
                h, t = items[i]
                n = 1 if t == NL else 5
                pe.wait_ge(a_ready, i + 1)
                if i >= 1:
                    pe.wait_ge(aT_ev, i)
                for j in range(n):
                    dst = ps[:, 4, j * P:(j + 1) * P] if j < 4 else ps[:, 5, 0:P]
                    last = pe.transpose(dst, am[i % 2][:, j * P:(j + 1) * P], ident[:, :])
                last.then_inc(aT_done, 1)

            def pv(i):
                h, t = items[i]
                pe.wait_ge(aT_ev, i + 1)
                if i >= 1:
                    pe.wait_ge(o_sq, i)
                slots = [5] if t == NL else range(5)
                for j, s in enumerate(slots):
                    last = mm(ps[:, 6, 0:P], aT[i % 2][:, j * P:(j + 1) * P],
                              vr[:, s, h * P:(h + 1) * P], j == 0, j == len(slots) - 1)
                last.then_inc(pv_done, 1)

            def trans_o(i):
                pe.wait_ge(on_ready, i + 1)
                if i >= 1:
                    pe.wait_ge(oT_ev, i)
                pe.transpose(ps[:, 7, 0:P], on[i % 2][:, :], ident[:, :]).then_inc(oT_done, 1)

            for i in range(NITEM + 5):
                if i < NITEM:
                    scores(i)
                if 2 <= i < NITEM + 2:
                    trans_a(i - 2)
                if 3 <= i < NITEM + 3:
                    pv(i - 3)
                if i >= 5:
                    trans_o(i - 5)

            pe.wait_ge(oT_ev, NITEM)
            pe.wait_ge(ld_wp, 32)
            for m in range(KD):
                if m % 2 == 0:
                    pe.wait_ge(ld_gate[m // 2], 32)
                cols = slice((m % 2) * P, (m % 2 + 1) * P)
                groups = [
                    (KD, lambda k: gate_w[m // 2][:, 0, k, cols], hT),
                    (H, lambda k: w_pa[:, k, m * P:(m + 1) * P], oT),
                    (KD, lambda k: gate_w[m // 2][:, 1, k, cols], hT),
                    (2, lambda k: w_pf[:, k, m * P:(m + 1) * P], fmT)]
                for j, (n, lhs, rhs) in enumerate(groups):
                    if m >= 1:
                        pe.wait_ge(sig_done if j % 2 == 0 else mg_ev, 2 * (m - 1) + j // 2 + 1)
                    for k in range(n):
                        mm(ps[:, 2 * j, :], lhs(k), rhs[:, k, 0:LAT], k == 0, k == n - 1)
                    for k in range(n):
                        last = mm(ps[:, 2 * j + 1, 0:P], lhs(k), rhs[:, k, LAT:TOK], k == 0, k == n - 1)
                    last.then_inc(mg_done, 1)
            pe.wait_ge(mg_ev, 2 * KD)
            for c in range(2):
                for k in range(KD):
                    last = pe.transpose(ps[:, 2 * c + k // 4, (k % 4) * P:(k % 4 + 1) * P],
                                        GG1[:, c, k:k + 1].to_broadcast([P, P]), ident[:, :])
                    if k == 0 and c == 0:
                        last.then_inc(mixer_gone, 1)
            last.then_inc(gg_done, 1)

            def out_proj(i):
                t = TILES[i]
                if i == 0:
                    pe.wait_ge(ld_wo, 16)
                    pe.wait_ge(gg_ev, 4)
                if i >= 2:
                    pe.wait_ge(y_used, i - 1)
                for n in range(2):
                    for k in range(KD):
                        last = mm(ps[:, 2 * (i % 2) + n, :], mT[:, k, t * P:(t + 1) * P],
                                  wo_sb[:, k, n * 512:(n + 1) * 512], k == 0, k == KD - 1)
                last.then_inc(y_done, 1)

            def x2_T_(i):
                pe.wait_ge(x2_ready, i + 1)
                if i >= 1:
                    pe.wait_ge(h2_a, i)
                    pe.wait_ge(h2_v, i)
                for k in range(KD):
                    last = pe.transpose(ps[:, 4 + k // 4, (k % 4) * P:(k % 4 + 1) * P],
                                        row[i % 2][:, k * P:(k + 1) * P], ident[:, :])
                last.then_inc(x2_T, 1)

            def router(i):
                if i == 0:
                    pe.wait_ge(ld_wr, 16)
                pe.wait_ge(h2_a, i + 1)
                pe.wait_ge(h2_v, i + 1)
                if i >= 1:
                    pe.wait_ge(lexp_ready, i)
                for k in range(KD):
                    last = mm(ps[:, 6, 0:E_], h2T[i % 2][:, k, :], w_r[:, k, :], k == 0, k == KD - 1)
                last.then_inc(lg_done, 1)

            def aff_T(i):
                t = TILES[i]
                pe.wait_ge(aff_ready, i + 1)
                if i == 1:
                    pe.wait_ge(affT_used, 1)
                dst = ps[0:E_, 7, 0:P] if t == NL else ps[0:E_, 7, t * P:(t + 1) * P]
                pe.transpose(dst, aff[i % 2][:, :], ident[:, :]).then_inc(affT_done, 1)

            for i in range(NT + 3):
                if i < NT:
                    out_proj(i)
                if 1 <= i < NT + 1:
                    x2_T_(i - 1)
                if 2 <= i < NT + 2:
                    router(i - 2)
                if i >= 3:
                    aff_T(i - 3)
            pe.wait_ge(top_ready, 1)
            pe.transpose(ps[0:CT, 5, 0:E_], topf[:, :], ident[0:E_, 0:E_])
            pe.transpose(ps[0:CT, 5, E_:2 * E_], topv[:, :], ident[0:E_, 0:E_]).then_inc(topT_done, 1)
            pe.wait_ge(idx_ready, 1)

            def split_product(e, n, out, lhs, first, last_):
                pe.wait_ge(w_lo_ready, e * NW + (n + 1))
                for a_ in range(2):
                    hi, lo = lhs(a_)
                    o_ = out(a_)
                    mm(o_, hi, w_hi[:, n % WB, a_, :], first(a_), False)
                    mm(o_, lo, w_hi[:, n % WB, a_, :], False, False)
                    ins = mm(o_, hi, w_lo[:, n % WB, a_, :], False, last_(a_))
                ins.then_inc(w_used, 1)

            def gate_up(e, s, q, n):
                if s >= 3 and q == 0:
                    pe.wait_ge(hid_ready, e * NS + (s - 2))
                split_product(e, n, lambda a_: ps[0:CT, s % 3, :],
                              lambda a_: (x_hi[:, 2 * q + a_, :], x_lo[:, 2 * q + a_, :]),
                              lambda a_: q == 0 and a_ == 0, lambda a_: q == KD // 2 - 1 and a_ == 1)

            def hid_T(e, s):
                pe.wait_ge(hid_ready, e * NS + (s + 1))
                if s >= 1:
                    pe.wait_ge(hT_lo_ready, e * NS + s)
                for f in range(2):
                    last = pe.transpose(ps[:, 7, f * CT:(f + 1) * CT], hid[s % 2][:, f * P:(f + 1) * P],
                                        ident[0:CT, 0:CT])
                last.then_inc(hidT_done, 1)

            def down(e, s, f, n):
                pe.wait_ge(hT_lo_ready, e * NS + (s + 1))
                if s == 0 and f == 0:
                    pe.wait_ge(yr_ready, e + 1)
                split_product(e, n, lambda a_: ps[0:CT, 5 + a_, :],
                              lambda a_: (h_hi[s % 2][:, f, :], h_lo[s % 2][:, f, :]),
                              lambda a_: s == 0 and f == 0, lambda a_: s == NS - 1 and f == 1)

            pe.sem_inc(w_used, WB)
            with pe.Fori(0, E_) as e:
                pe.wait_ge(gathered, (e + 1) * 16)
                for k in range(KD):
                    last = pe.transpose(ps[:, 3 + k // 4, (k % 4) * CT:(k % 4 + 1) * CT], xe[:, k * P:(k + 1) * P],
                                        ident[0:CT, 0:CT])
                last.then_inc(xeT_done, 1)
                pe.wait_ge(xeT_ev, e + 1)
                n = 0
                for s, units in enumerate(STEPS):
                    for kind, us, q in units:
                        if kind == "gu":
                            gate_up(e, us, q, n)
                            n += 1
                    if 1 <= s < NS + 1:
                        hid_T(e, s - 1)
                    for kind, us, q in units:
                        if kind == "d":
                            down(e, us, q, n)
                            n += 1
            pe.wait_ge(yr_ready, E_ + 1)
            for c in range(2):
                for k in range(KD):
                    last = pe.transpose(ps[:, 2 * c + k // 4, (k % 4) * P:(k % 4 + 1) * P],
                                        GG2[:, c, k:k + 1].to_broadcast([P, P]), ident[:, :])
            last.then_inc(gg2_done, 1)

        @block.scalar
        def _(act):
            for t in TILES:
                act.wait_ge(ld_x[t], 16)
                act.activation(xn[:, t, :], x1[:, t, :], ACT.Square, accum_out=ssx[:, t:t + 1]).then_inc(x_sq, 1)
            act.wait_ge(par_ready, 1)
            act.activation(sil_c[:, :, :], pT[:, C_COL:C_COL + 16].rearrange("p (c k) -> p c k", c=2),
                           ACT.Silu).then_inc(silu_ready, 1)
            act.wait_ge(lam_sum, 2)
            act.activation(lexp[:, :], lsum[:, :], ACT.Exp).then_inc(lam_exp, 1)

            act.wait_ge(mod1_ready, 1)
            act.wait_ge(xT_ctx, 1)
            for k in range(4, KD):
                last = act.activation(hT[:, k, LAT:TOK], ps[:, 4 + k // 4, (k % 4) * P:(k % 4 + 1) * P], ACT.Identity,
                                      bias=modT[:, SH1 + k, 1:2], scale=A1[:, 1, k:k + 1])
            last.then_inc(h_odd, 1)
            for k in range(1, KD, 2):
                act.wait_ge(xT_lat, k + 1)
                act.activation(hT[:, k, 0:LAT], ps[:, k % 4, :], ACT.Identity, bias=modT[:, SH1 + k, 0:1],
                               scale=A1[:, 0, k:k + 1]).then_inc(h_odd, 1)

            def t_copy(j):
                act.wait_ge(t_done, j + 1)
                b = ps[:, 4 + j % 2, 0:HALF].rearrange("p (h t) -> p h t", h=3)
                if j >= len(QK):
                    h0 = 3 * (j - len(QK))
                    act.activation(kT[:, h0:h0 + 3, 0:P], b, ACT.Copy).then_inc(t_ev, 1)
                    return
                kind, _, half, t = UNITS[QK[j]]
                h0 = 3 * half
                if kind == "q":
                    act.activation(qT[:, h0:h0 + 3, t * P:(t + 1) * P], b, ACT.Copy, scale=DH ** -0.5).then_inc(t_ev, 1)
                else:
                    act.activation(kT[:, h0:h0 + 3, P + t * P:2 * P + t * P], b, ACT.Copy).then_inc(t_ev, 1)

            act.wait_ge(scattered, 16 * NT)
            for u, (kind, n, half, t) in enumerate(UNITS):
                if kind == "f" or kind == "v" or t == NL:
                    act.wait_ge(z_done, u + 1)
                if kind == "f":
                    c0, c1 = (0, LAT) if t < NL else (LAT, TOK)
                    act.activation(fT[:, half, c0:c1], ps[:, u % 4, 0:c1 - c0], ACT.Copy).then_inc(z_act, 1)
                elif kind == "v":
                    act.activation(vr[:, t + 1, half * HALF:(half + 1) * HALF], ps[:, u % 4, 0:HALF],
                                   ACT.Copy).then_inc(z_act, 1)
                elif t == NL:
                    j = QK.index(u)
                    if j >= 3:
                        act.wait_ge(t_done, j - 2)
                    act.activation(zr[j % 3][:, :], ps[:, u % 4, 0:HALF], ACT.Copy).then_inc(z_act, 1)
                if u - 1 in QK:
                    t_copy(QK.index(u - 1))
            for j in range(len(QK), NTR):
                t_copy(j)
            for c in range(2):
                act.wait_ge(fm_done, c + 1)
                act.activation(fmT[:, c, 0:LAT], ps[:, c, :], ACT.Copy).then_inc(fm_ev, 1)
            for c in range(2):
                act.wait_ge(fm_done, c + 3)
                act.activation(fmT[:, c, LAT:TOK], ps[:, 2 + c, 0:CTX], ACT.Copy).then_inc(fm_ev, 1)

            def exps(i):
                w = CTX if items[i][1] == NL else P + LAT
                for c in range(2):
                    n = 2 * i + c
                    act.wait_ge(negm_ready, n + 1)
                    if n >= 4:
                        act.wait_ge(a_ready, (n - 4) // 2 + 1)
                    b = 2 * (n % 2)
                    act.activation(pr[n % 4][:, 0:w], ps[:, b:b + 2, :].rearrange("p b n -> p (b n)")[:, 0:w], ACT.Exp,
                                   bias=negm[:, n:n + 1], accum_out=psumr[:, n:n + 1]).then_inc(p_ready, 1)

            def a_copy(i):
                act.wait_ge(aT_done, i + 1)
                if i >= 2:
                    act.wait_ge(pv_done, i - 1)
                w = CTX if items[i][1] == NL else LAT
                last = act.activation(aT[i % 2][:, 0:w], ps[:, 4, 0:w], ACT.Copy)
                if w == LAT:
                    last = act.activation(aT[i % 2][:, LAT:LAT + P], ps[:, 5, 0:P], ACT.Copy)
                last.then_inc(aT_ev, 1)

            def o_square(i):
                act.wait_ge(pv_done, i + 1)
                if i >= 3:
                    act.wait_ge(on_ready, i - 2)
                act.activation(orow[i % 3][:, :], ps[:, 6, 0:P], ACT.Copy).then_inc(o_rows, 1)
                act.activation(ojunk[:, :], ps[:, 6, 0:P], ACT.Square, accum_out=oss[:, i:i + 1]).then_inc(o_sq, 1)

            def o_copy(i):
                h, t = items[i]
                act.wait_ge(oT_done, i + 1)
                act.activation(oT[:, h, t * P:(t + 1) * P], ps[:, 7, 0:P], ACT.Copy,
                               scale=gsub[:, 0:1]).then_inc(oT_ev, 1)

            for i in range(NITEM + 6):
                if 4 <= i < NITEM + 4:
                    o_square(i - 4)
                if i < NITEM:
                    exps(i)
                if 2 <= i < NITEM + 2:
                    a_copy(i - 2)
                if i >= 6:
                    o_copy(i - 6)

            for m in range(KD):
                for g in range(2):
                    buf = (sg_a, sg_f)[g]
                    act.wait_ge(mg_done, 4 * m + 2 * g + 1)
                    if m >= 1:
                        act.wait_ge(mg_ev, 2 * (m - 1) + g + 1)
                    act.activation(buf[:, 0:LAT], ps[:, 4 * g, :], ACT.Sigmoid)
                    act.activation(buf[:, LAT:TOK], ps[:, 4 * g + 1, 0:P], ACT.Sigmoid).then_inc(sig_done, 1)
            act.wait_ge(gg_done, 1)
            for b in range(4):
                act.activation(ggrow[:, b // 2, (b % 2) * 512:(b % 2 + 1) * 512], ps[:, b, :], ACT.Copy).then_inc(gg_ev, 1)

            def y_square(i):
                act.wait_ge(y_done, i + 1)
                if i >= 2:
                    act.wait_ge(x2_T, i - 1)
                    act.wait_ge(x2_stored[i % 2], 16 * (i // 2))
                b = 2 * (i % 2)
                act.activation(row[i % 2][:, :], ps[:, b:b + 2, :].rearrange("p b n -> p (b n)"), ACT.Square,
                               accum_out=ssy[:, i:i + 1]).then_inc(y_sq, 1)

            def x1_square(i):
                act.wait_ge(x1_ready, i + 1)
                act.activation(row[i % 2][:, :], x1[:, TILES[i], :], ACT.Square,
                               accum_out=ss2[:, i:i + 1]).then_inc(x1_sq, 1)

            def h2_high(i):
                c = cond(TILES[i])
                act.wait_ge(x2_T, i + 1)
                if i >= 2:
                    act.wait_ge(lg_done, i - 1)
                for k in range(4, KD):
                    last = act.activation(h2T[i % 2][:, k, :], ps[:, 4 + k // 4, (k % 4) * P:(k % 4 + 1) * P],
                                          ACT.Identity, bias=modT[:, SH2 + k, c:c + 1], scale=A2[:, c, k:k + 1])
                last.then_inc(h2_a, 1)

            def l_exp(i):
                act.wait_ge(lneg_ready, i + 1)
                if i >= 2:
                    act.wait_ge(affT_done, i - 1)
                act.activation(aff[i % 2][:, :], ps[:, 6, 0:E_], ACT.Exp, bias=lneg[:, i:i + 1],
                               accum_out=lden[:, i:i + 1]).then_inc(lexp_ready, 1)

            for i in range(NT + 2):
                if i < NT:
                    y_square(i)
                    x1_square(i)
                if 1 <= i < NT + 1:
                    h2_high(i - 1)
                if i >= 2:
                    l_exp(i - 2)

            act.wait_ge(idx_ready, 1)
            act.sem_inc(yr_ready, 1)

            def ring_wait(e, kind, s, q):
                if kind == "gu" and q == 0:
                    for j in (2 * s, 2 * s + 1):
                        act.wait_ge(gu_ld[j % GUR], e * 32 + 16 * (j // GUR + 1))
                if kind == "d":
                    j = 2 * s + q
                    act.wait_ge(d_ld[j % DR], e * 32 + 16 * (j // DR + 1))

            with act.Fori(0, E_) as e:
                n = 0
                for s, units in enumerate(STEPS):
                    for x in range(max(len(units), 2)):
                        if x == 2 or len(units) == 2 and x == 0:
                            if 1 <= s < NS + 1:
                                act.wait_ge(w_used, e * NW + (gu_end[s - 1] + WB))
                                act.activation(sil[(s - 1) % 2][:, :], ps[0:CT, (s - 1) % 3, gate_cols(s - 1)[0]],
                                               ACT.Silu).then_inc(sil_ready, 1)
                            if s >= 2:
                                act.wait_ge(hidT_done, e * NS + (s - 1))
                                if s >= 4:
                                    act.wait_ge(w_used, e * NW + (d_end[s - 4] + WB))
                                act.activation(h_hi[s % 2][:, :, :].rearrange("p f c -> p (f c)"), ps[:, 7, 0:2 * CT],
                                               ACT.Copy).then_inc(hT_hi_ready, 1)
                        if x < len(units):
                            ring_wait(e, *units[x])
                            act.wait_ge(w_used, e * NW + (n + 1))
                            act.activation(unit_dst(w_hi, units[x], n), unit_src(units[x]), ACT.Copy).then_inc(w_hi_ready, 1)
                            n += 1
                act.wait_ge(w_used, e * NW + (NW + WB))
                act.wait_ge(scattered, (e + NT) * 16)
                act.activation(yr[:, :], ps[0:CT, 5:7, :].rearrange("p b n -> p (b n)"), ACT.Copy,
                               scale=gT[:, bass.ds(e, 1)]).then_inc(yr_ready, 1)
            act.wait_ge(gg2_done, 1)
            for b in range(4):
                act.activation(ggrow2[:, b // 2, (b % 2) * 512:(b % 2 + 1) * 512], ps[:, b, :],
                               ACT.Copy).then_inc(gg2_ev, 1)
            for t in range(NT):
                act.wait_ge(ld_fin[t], 16)
                act.activation(fout[:, t, :], fin[:, t, :], ACT.Square, accum_out=ssx[:, t:t + 1]).then_inc(f_sq, 1)

        @block.vector
        def _(dve):
            steps = [0]

            def link(ins):
                steps[0] += 1
                ins.then_inc(v_chain, 1)
                dve.wait_ge(v_chain, steps[0])

            dve.wait_ge(par_T, 1)
            dve.tensor_copy(pT[:, :], ps[:, 7, 384:384 + 97]).then_inc(par_ready, 1)
            for t in TILES:
                dve.wait_ge(x_rs, TILES.index(t) + 1)
                dve.tensor_scalar(xn[:, t, :], x1[:, t, :], rsx[:, t:t + 1], None, ALU.mult).then_inc(xn_ready, 1)
            dve.wait_ge(par_ready, 1)
            dve.tensor_scalar(gsub[:, :], pT[:, 96:97], 1.0 - LAM_INIT, None, ALU.mult)
            dve.wait_ge(ld_lam, 64)
            for i in range(2):
                dve.tensor_tensor_reduce(zt[:, DH * i:DH * (i + 1)], lamv[:, 2 * i, :], lamv[:, 2 * i + 1, :], 1.0, 0.0,
                                         ALU.mult, ALU.add, lsum[:, i:i + 1]).then_inc(lam_sum, 1)
            dve.wait_ge(lam_exp, 1)
            dve.tensor_scalar(nlam[:, :], lexp[:, 1:2], lexp[:, 0:1], LAM_INIT, ALU.subtract, ALU.subtract)

            def gain(out, col, gcol, plus):
                for c in range(2):
                    last = dve.scalar_tensor_tensor(out[:, c, :], modT[:, col:col + KD, c], plus,
                                                    pT[:, gcol:gcol + KD], ALU.add, ALU.mult)
                return last

            def mod_copy(m0, m1):
                return dve.tensor_tensor(modT[:, m0:m1, :],
                                         ps[:, 7, 256 + 2 * m0:256 + 2 * m1].rearrange("p (m c) -> p m c", c=2),
                                         pT[:, m0:m1].unsqueeze(2).to_broadcast([P, m1 - m0, 2]), ALU.add)

            dve.wait_ge(mod_done, 4)
            link(mod_copy(0, 2 * KD))
            gain(A1, SC1, G_PRE_MIX, 1.0).then_inc(mod1_ready, 1)
            dve.wait_ge(mod1_ready, 1)
            dve.wait_ge(xT_ctx, 1)
            for k in range(4):
                last = dve.tensor_scalar(hT[:, k, LAT:TOK], ps[:, 4 + k // 4, (k % 4) * P:(k % 4 + 1) * P],
                                         A1[:, 1, k:k + 1], modT[:, SH1 + k, 1:2], ALU.mult, ALU.add)
            last.then_inc(h_even, 1)
            for k in range(0, KD, 2):
                dve.wait_ge(xT_lat, k + 1)
                dve.tensor_scalar(hT[:, k, 0:LAT], ps[:, k % 4, :], A1[:, 0, k:k + 1], modT[:, SH1 + k, 0:1],
                                  ALU.mult, ALU.add).then_inc(h_even, 1)

            dve.wait_ge(ld_tab, 16)
            for j, u in enumerate(QK):
                kind, n, half, t = UNITS[u]
                if t == NL:
                    continue
                dve.wait_ge(z_done, u + 1)
                if j >= 3:
                    dve.wait_ge(t_done, j - 2)
                    if UNITS[QK[j - 3]][0] == "k" and UNITS[QK[j - 3]][3] == NL:
                        dve.wait_ge(nk_stored, 16 * ((j - 3) // NT + 1))
                b = ps[:, u % 4, 0:HALF]
                z = zr[j % 3]
                cos = rope[:, t, 0, :].unsqueeze(1).to_broadcast([P, 6, DH])
                dve.tensor_tensor(z[:, :].rearrange("p (g d) -> p g d", d=DH), b.rearrange("p (g d) -> p g d", d=DH),
                                  cos, ALU.mult)
                b5 = b.rearrange("p (g a b i) -> p g a b i", g=6, a=2, b=2)
                t5 = zt[:, :].rearrange("p (g a b i) -> p g a b i", g=6, a=2, b=2)
                if ev_of[u][1] > 1:
                    dve.wait_ge(z_dve, ev_of[u][1] - 1)
                s4 = rope[:, t, 1, :].rearrange("p (a b i) -> p a b i", a=2, b=2)
                for x in range(2):
                    last = dve.tensor_tensor(t5[:, :, :, x, :], b5[:, :, :, 1 - x, :],
                                             s4[:, :, x, :].unsqueeze(1).to_broadcast([P, 6, 2, DH // 4]), ALU.mult)
                link(last)
                dve.tensor_tensor(z[:, :], z[:, :], zt[:, :], ALU.add).then_inc(z_dve, 1)
            dve.wait_ge(mod_done, 12)
            link(mod_copy(2 * KD, NMOD * KD))
            gain(A2, SC2, G_PRE_FFN, 1.0)
            gain(GG1, GT1, G_POST_MIX, 0.0)
            gain(GG2, GT2, G_POST_FFN, 0.0).then_inc(mod2_ready, 1)
            g = 0
            for t in range(NT):
                for c in range(2):
                    dve.wait_ge(g_done, g + 1)
                    dve.tensor_copy(Gs[:, t, c, :], ps[:, 4 + g % 3, 0:256]).then_inc(g_ev, 1)
                    g += 1

            def maxima(i):
                w = CTX if items[i][1] == NL else P + LAT
                for c in range(2):
                    n = 2 * i + c
                    dve.wait_ge(s_done, n + 1)
                    b = 2 * (n % 2)
                    dve.tensor_reduce(negm[:, n:n + 1], ps[:, b:b + 2, :].rearrange("p b n -> p (b n)")[:, 0:w], AXX,
                                      ALU.max, negate=True).then_inc(negm_ready, 1)

            def combine(i):
                w = CTX if items[i][1] == NL else P + LAT
                n = 2 * i
                dve.wait_ge(p_ready, n + 2)
                link(dve.reciprocal(rs[:, n:n + 2], psumr[:, n:n + 2]))
                link(dve.tensor_tensor(nl[:, i:i + 1], rs[:, n + 1:n + 2], nlam[:, :], ALU.mult))
                link(dve.tensor_scalar(pr[(n + 1) % 4][:, 0:w], pr[(n + 1) % 4][:, 0:w], nl[:, i:i + 1], None, ALU.mult))
                if i >= 2:
                    dve.wait_ge(aT_done, i - 1)
                dve.scalar_tensor_tensor(am[i % 2][:, 0:w], pr[n % 4][:, 0:w], rs[:, n:n + 1], pr[(n + 1) % 4][:, 0:w],
                                         ALU.mult, ALU.add).then_inc(a_ready, 1)

            def o_norm(i):
                dve.wait_ge(o_rs, i + 1)
                if i >= 2:
                    dve.wait_ge(oT_done, i - 1)
                dve.tensor_scalar(on[i % 2][:, :], orow[i % 3][:, :], ort[:, i:i + 1], None,
                                  ALU.mult).then_inc(on_ready, 1)

            for i in range(NITEM + 5):
                if i < NITEM:
                    maxima(i)
                if 1 <= i < NITEM + 1:
                    combine(i - 1)
                if i >= 5:
                    o_norm(i - 5)

            for m in range(KD):
                for g, (buf, out) in enumerate(((sg_a, t_pa), (sg_f, sg_f))):
                    if m >= 1 and g == 0:
                        dve.wait_ge(mg_ev, 2 * m)
                    dve.wait_ge(sig_done, 2 * m + g + 1)
                    dve.wait_ge(mg_done, 4 * m + 2 * g + 2)
                    dve.tensor_tensor(out[:, 0:LAT], buf[:, 0:LAT], ps[:, 4 * g + 2, :], ALU.mult)
                    last = dve.tensor_tensor(out[:, LAT:TOK], buf[:, LAT:TOK], ps[:, 4 * g + 3, 0:P], ALU.mult)
                    if g == 0:
                        last.then_inc(mg_ev, 1)
                link(last)
                dve.tensor_tensor(mT[:, m, :], t_pa[:, :], sg_f[:, :], ALU.add).then_inc(mg_ev, 1)

            def residual(i):
                t = TILES[i]
                b = 2 * (i % 2)
                if i == 0:
                    dve.wait_ge(gg_ev, 4)
                dve.wait_ge(y_rs, i + 1)
                dve.scalar_tensor_tensor(row[i % 2][:, :], ps[:, b:b + 2, :].rearrange("p b n -> p (b n)"),
                                         rsy[:, i:i + 1], ggrow[:, cond(t), :], ALU.mult, ALU.mult).then_inc(y_used, 1)
                dve.wait_ge(y_used, i + 1)
                dve.tensor_tensor(x1[:, t, :], x1[:, t, :], row[i % 2][:, :], ALU.add).then_inc(x1_ready, 1)
                dve.wait_ge(x1_rs, i + 1)
                dve.tensor_scalar(row[i % 2][:, :], x1[:, t, :], rs2[:, i:i + 1], None, ALU.mult).then_inc(x2_ready, 1)

            def h2_low(i):
                c = cond(TILES[i])
                dve.wait_ge(x2_T, i + 1)
                if i >= 2:
                    dve.wait_ge(lg_done, i - 1)
                for k in range(4):
                    last = dve.tensor_scalar(h2T[i % 2][:, k, :], ps[:, 4 + k // 4, (k % 4) * P:(k % 4 + 1) * P],
                                             A2[:, c, k:k + 1], modT[:, SH2 + k, c:c + 1], ALU.mult, ALU.add)
                last.then_inc(h2_v, 1)

            def l_max(i):
                dve.wait_ge(lg_done, i + 1)
                dve.tensor_reduce(lneg[:, i:i + 1], ps[:, 6, 0:E_], AXX, ALU.max, negate=True).then_inc(lneg_ready, 1)

            def affinity(i):
                dve.wait_ge(lexp_ready, i + 1)
                link(dve.reciprocal(lrec[:, i:i + 1], lden[:, i:i + 1]))
                dve.tensor_scalar(aff[i % 2][:, :], aff[i % 2][:, :], lrec[:, i:i + 1], None,
                                  ALU.mult).then_inc(aff_ready, 1)

            def choose(work, n, c0, cap):
                for r in range(cap // 8):
                    v8, i8 = topv[:, c0 + 8 * r:c0 + 8 * r + 8], topi[:, c0 + 8 * r:c0 + 8 * r + 8]
                    link(dve.max(v8, work[:, 0:n]))
                    link(dve.max_index(i8, v8, work[:, 0:n]))
                    if r < cap // 8 - 1:
                        link(dve.match_replace(work[:, 0:n], v8, work[:, 0:n], -1.0))

            for i in range(NT + 3):
                if i < NT:
                    residual(i)
                if i == 3:
                    dve.wait_ge(affT_done, 1)
                    dve.tensor_copy(work_c[:, :], ps[0:E_, 7, 0:P]).then_inc(affT_used, 1)
                if 1 <= i < NT + 1:
                    h2_low(i - 1)
                if 2 <= i < NT + 2:
                    l_max(i - 2)
                    affinity(i - 2)
            dve.wait_ge(affT_used, 1)
            choose(work_c, CTX, CL, CC)
            dve.wait_ge(affT_done, NT)
            link(dve.tensor_copy(work[:, :], ps[0:E_, 7, :]))
            choose(work, LAT, 0, CL)
            dve.tensor_copy(topf[:, 0:CL], topi[:, 0:CL])
            dve.tensor_scalar(topf[:, CL:CT], topi[:, CL:CT], float(LAT), None, ALU.add).then_inc(top_ready, 1)
            dve.wait_ge(topT_done, 1)
            dve.tensor_copy(idxT[:, :], ps[0:CT, 5, 0:E_])
            dve.tensor_copy(gT[:, :], ps[0:CT, 5, E_:2 * E_]).then_inc(idx_ready, 1)

            dve.wait_ge(idx_ready, 1)
            with dve.Fori(0, E_) as e:
                dve.wait_ge(xeT_done, e + 1)
                for c, (c0, c1) in enumerate(((0, CL), (CL, CT))):
                    src = ps[:, 3:5, 0:4 * CT].rearrange("p b (k c) -> p b k c", k=4)[:, :, :, c0:c1]
                    dst = xeT[:, :, :].rearrange("p (b k) c -> p b k c", b=2)[:, :, :, c0:c1]
                    gain_ = A2[:, c, :].rearrange("p (b k) -> p b k", b=2).unsqueeze(3).to_broadcast([P, 2, 4, c1 - c0])
                    dve.tensor_tensor(dst, src, gain_, ALU.mult).then_inc(v_loop, 1)
                dve.wait_ge(v_loop, e * 2 + 2)
                for c, (c0, c1) in enumerate(((0, CL), (CL, CT))):
                    dst = xeT[:, :, c0:c1]
                    shift = modT[:, SH2:SH2 + KD, c:c + 1].to_broadcast([P, KD, c1 - c0])
                    last = dve.tensor_tensor(dst, dst, shift, ALU.add)
                last.then_inc(x_hi_ready, 1)
                dve.wait_ge(x_hi_ready, e * 2 + 1)
                dve.tensor_copy(x_hi[:, :, :], xeT[:, :, :]).then_inc(x_hi_ready, 1)
                dve.wait_ge(x_hi_ready, e * 2 + 2)
                dve.tensor_tensor(x_lo[:, :, :], xeT[:, :, :], x_hi[:, :, :].bitcast(F32), ALU.subtract).then_inc(xeT_ev, 1)
                n = 0
                for s, units in enumerate(STEPS):
                    for x in range(max(len(units), 2)):
                        if x == 2 or len(units) == 2 and x == 0:
                            if 1 <= s < NS + 1:
                                dve.wait_ge(sil_ready, e * NS + s)
                                if s >= 3:
                                    dve.wait_ge(hidT_done, e * NS + (s - 2))
                                dve.tensor_tensor(hid[(s - 1) % 2][:, :], sil[(s - 1) % 2][:, :],
                                                  ps[0:CT, (s - 1) % 3, gate_cols(s - 1)[1]],
                                                  ALU.mult).then_inc(hid_ready, 1)
                            if s >= 2:
                                dve.wait_ge(hT_hi_ready, e * NS + (s - 1))
                                dve.tensor_tensor(h_lo[s % 2][:, :, :].rearrange("p f c -> p (f c)"), ps[:, 7, 0:2 * CT],
                                                  h_hi[s % 2][:, :, :].rearrange("p f c -> p (f c)").bitcast(F32),
                                                  ALU.subtract).then_inc(hT_lo_ready, 1)
                        if x < len(units):
                            kind, us, q = units[x]
                            dve.wait_ge(w_hi_ready, e * NW + (n + 1))
                            ins = dve.tensor_tensor(unit_dst(w_lo, units[x], n), unit_src(units[x]),
                                                    unit_dst(w_hi, units[x], n).bitcast(F32), ALU.subtract)
                            ins.then_inc(w_lo_ready, 1)
                            n += 1

            dve.wait_ge(gg2_ev, 4)
            for t in range(NT):
                dve.wait_ge(f_rs, t + 1)
                link(dve.scalar_tensor_tensor(fout[:, t, :], fin[:, t, :], rsx[:, t:t + 1], ggrow2[:, cond(t), :],
                                              ALU.mult, ALU.mult))
                dve.tensor_tensor(fout[:, t, :], fout[:, t, :], x1[:, t, :], ALU.add).then_inc(f_ready, 1)


_INS = ["x_prompt", "x_sample", "c", "cache_k", "cache_v", "c_ctx", "w_mod", "b_mod", "g_pre_mix", "g_post_mix",
        "g_pre_ffn", "g_post_ffn", "w_in", "lam_q1", "lam_k1", "lam_q2", "lam_k2", "g_subln", "w_proj_attn",
        "w_proj_fourier", "w_out", "w_router", "w_gate", "w_up", "w_down"]
_OUTS = [(1, CTX, D), (1, LAT, D), (1, 1, H, CTX, 2 * DH), (1, 1, H, CTX, 2 * DH)]


def kernel(**inputs):
    import concourse.bacc as _bacc
    from concourse.bass_utils import run_bass_kernel_spmd as _run

    nc = _bacc.Bacc("TRN2", target_bir_lowering=False, num_devices=1)
    arrays, aps = {}, {}
    given = {n: np.ascontiguousarray(inputs[n]) for n in _INS}
    given.update({n: np.ascontiguousarray(v, dtype=np.float32) for n, v in constants().items()})
    for name, v in given.items():
        arrays[f"in_{name}"] = v
        aps[name] = nc.dram_tensor(f"in_{name}", v.shape, F32, kind="ExternalInput").ap()
    outs = [nc.dram_tensor(f"out_{i}", s, F32, kind="ExternalOutput").ap() for i, s in enumerate(_OUTS)]
    program(nc, aps, outs)
    r = _run(nc, [arrays], core_ids=[0])
    return tuple(r.results[0][f"out_{i}"] for i in range(len(_OUTS)))
```
